# Optimizing a Trainium2 kernel written in Bass

```python
import jax, jax.numpy as jnp
from jax import lax
import numpy as np

D_MODEL = 1024
BATCH = 1
SEQ = 512
DEPTH = 2

PLE_DIM = 256
EPS = 1e-6

A_GROUPS = 8
A_WIDTH = D_MODEL
CONV_WIDTH = 3
B_GROUPS = 8
B_WIDTH = D_MODEL
B_GDIM = B_WIDTH // B_GROUPS
B_CHUNK = 128
EVEN_IN = 4 * A_WIDTH + 3 * B_WIDTH
EVEN_MIX = A_WIDTH + B_WIDTH
EVEN_SPLITS = [A_WIDTH, 2 * A_WIDTH, 3 * A_WIDTH, 4 * A_WIDTH,
               4 * A_WIDTH + B_WIDTH, 4 * A_WIDTH + 2 * B_WIDTH]

C_HEADS = 8
C_DQK = D_MODEL // C_HEADS
C_DV = 2 * D_MODEL // C_HEADS
C_QK = C_HEADS * C_DQK
C_WIDTH = C_HEADS * C_DV
C_CHUNK = 128
ODD_IN = 2 * C_QK + 3 * C_WIDTH + 2 * C_HEADS
ODD_SPLITS = [C_QK, 2 * C_QK, 2 * C_QK + C_WIDTH, 2 * C_QK + 2 * C_WIDTH, 2 * C_QK + 3 * C_WIDTH]

N_EVEN = (DEPTH + 1) // 2
N_ODD = DEPTH // 2

kernel_name = 'hybrid_conv_gmlp_mlstm_trunk'

def rmsnorm(x, g):
    xf = x.astype(jnp.float32)
    y = xf * lax.rsqrt(jnp.mean(xf * xf, axis=-1, keepdims=True) + EPS)
    return (y * g.astype(jnp.float32)).astype(x.dtype)

def layernorm(x, g, b):
    xf = x.astype(jnp.float32)
    mu = jnp.mean(xf, axis=-1, keepdims=True)
    xc = xf - mu
    y = xc * lax.rsqrt(jnp.mean(xc * xc, axis=-1, keepdims=True) + EPS)
    return (y * g.astype(jnp.float32) + b.astype(jnp.float32)).astype(x.dtype)

def causal_short_conv(z, w):
    seq = z.shape[1]
    zp = jnp.pad(z, ((0, 0), (CONV_WIDTH - 1, 0), (0, 0)))
    out = w[CONV_WIDTH - 1] * z
    for j in range(CONV_WIDTH - 1):
        out = out + w[j] * zp[:, j:j + seq]
    return out

def conv_gmlp_mixer(xn, w_in, conv_w, ln_g, ln_b, w_s, b_s, w_out):
    bsz, seq, _ = xn.shape
    n_chunks = seq // B_CHUNK
    proj = xn @ w_in
    a_b, a_c, a_x, a_gate, b_u, b_v, b_gate = jnp.split(proj, EVEN_SPLITS, axis=-1)
    y_a = a_b * causal_short_conv(a_c * a_x, conv_w) * jax.nn.silu(a_gate)
    v = layernorm(b_v, ln_g, ln_b).reshape(bsz, n_chunks, B_CHUNK, B_GROUPS, B_GDIM)
    causal = jnp.tril(jnp.ones((B_CHUNK, B_CHUNK), dtype=bool))
    w_causal = jnp.where(causal, w_s, jnp.zeros_like(w_s))
    s = jnp.einsum('gts,bnsgc->bntgc', w_causal, v) + b_s[None, None, :, :, None]
    y_b = b_u * s.reshape(bsz, seq, B_WIDTH) * jax.nn.silu(b_gate)
    return jnp.concatenate([y_a, y_b], axis=-1) @ w_out

def mlstm_mixer(xn, w_in, b_if, mh_g, w_out):
    bsz, seq, _ = xn.shape
    nc, L, H = seq // C_CHUNK, C_CHUNK, C_HEADS
    f32 = jnp.float32
    proj = xn @ w_in
    q, k, v, o, z, gif = jnp.split(proj, ODD_SPLITS, axis=-1)
    gif = gif.astype(f32) + b_if.astype(f32)
    i_pre = gif[..., :H].reshape(bsz, nc, L, H)
    log_f = jax.nn.log_sigmoid(gif[..., H:]).reshape(bsz, nc, L, H)
    q = q.astype(f32).reshape(bsz, nc, L, H, C_DQK) * (C_DQK ** -0.5)
    k = k.astype(f32).reshape(bsz, nc, L, H, C_DQK)
    v = v.astype(f32).reshape(bsz, nc, L, H, C_DV)

    b = jnp.cumsum(log_f, axis=2)
    g = b[:, :, -1]
    a = g[:, :, None] - b + i_pre

    def chunk_step(carry, xs):
        c_st, n_st, m_st = carry
        k_c, v_c, a_c, g_c = xs
        m_new = jnp.maximum(g_c + m_st, jnp.max(a_c, axis=1))
        decay = jnp.exp(g_c + m_st - m_new)
        w = jnp.exp(a_c - m_new[:, None])
        c_new = decay[..., None, None] * c_st + jnp.einsum('blh,blhk,blhv->bhkv', w, k_c, v_c)
        n_new = decay[..., None] * n_st + jnp.einsum('blh,blhk->bhk', w, k_c)
        return (c_new, n_new, m_new), (c_st, n_st, m_st)

    init = (jnp.zeros((bsz, H, C_DQK, C_DV), f32), jnp.zeros((bsz, H, C_DQK), f32),
            jnp.zeros((bsz, H), f32))
    xs = (jnp.moveaxis(k, 1, 0), jnp.moveaxis(v, 1, 0), jnp.moveaxis(a, 1, 0), jnp.moveaxis(g, 1, 0))
    _, (c_all, n_all, m_all) = lax.scan(chunk_step, init, xs)
    c_all = jnp.moveaxis(c_all, 0, 1)
    n_all = jnp.moveaxis(n_all, 0, 1)
    m_all = jnp.moveaxis(m_all, 0, 1)

    bt = jnp.moveaxis(b, 3, 2)
    it = jnp.moveaxis(i_pre, 3, 2)
    causal = jnp.tril(jnp.ones((L, L), dtype=bool))
    d = jnp.where(causal, bt[..., :, None] - bt[..., None, :] + it[..., None, :], -jnp.inf)
    m_inter = bt + m_all[..., None]
    m_t = jnp.maximum(m_inter, jnp.max(d, axis=-1))
    p_mat = jnp.exp(d - m_t[..., None]) * jnp.einsum('bnthk,bnshk->bnhts', q, k)
    inter_scale = jnp.exp(m_inter - m_t)
    num = (inter_scale[..., None] * jnp.einsum('bnthk,bnhkv->bnhtv', q, c_all)
           + jnp.einsum('bnhts,bnshv->bnhtv', p_mat, v))
    den = inter_scale * jnp.einsum('bnthk,bnhk->bnht', q, n_all) + jnp.sum(p_mat, axis=-1)
    hc = num / jnp.maximum(jnp.abs(den), jnp.exp(-m_t))[..., None]
    hc = hc * lax.rsqrt(jnp.mean(hc * hc, axis=-1, keepdims=True) + EPS) * mh_g.astype(f32)[:, None, :]
    hc = jnp.moveaxis(hc, 2, 3).reshape(bsz, seq, C_WIDTH).astype(xn.dtype)
    y = hc * jax.nn.sigmoid(o) * jax.nn.silu(z)
    return y @ w_out

def setup_inputs(seed: int = 0) -> dict:
    key = jax.random.key(seed)
    ks = jax.random.split(key, 20)

    def nrm(k, shape, scale):
        return scale * jax.random.normal(k, shape, jnp.float32)

    f_bias = jnp.linspace(3.0, 6.0, C_HEADS, dtype=jnp.float32)
    b_if = jnp.concatenate([nrm(ks[16], (N_ODD, C_HEADS), 0.1),
                            f_bias[None, :] + nrm(ks[17], (N_ODD, C_HEADS), 0.1)], axis=-1)
    return {
        'x': nrm(ks[0], (BATCH, SEQ, D_MODEL), 1.0),
        'p': nrm(ks[1], (DEPTH, BATCH, SEQ, PLE_DIM), 1.0),
        'pre_g': 1.0 + nrm(ks[2], (DEPTH, D_MODEL), 0.02),
        'post_g': 1.0 + nrm(ks[3], (DEPTH, D_MODEL), 0.02),
        'ple_g': 1.0 + nrm(ks[4], (DEPTH, D_MODEL), 0.02),
        'w_ple': nrm(ks[5], (DEPTH, PLE_DIM, D_MODEL), PLE_DIM ** -0.5),
        'w_ple_gate': nrm(ks[6], (DEPTH, D_MODEL, D_MODEL), D_MODEL ** -0.5),
        'even_w_in': nrm(ks[7], (N_EVEN, D_MODEL, EVEN_IN), D_MODEL ** -0.5),
        'even_conv_w': nrm(ks[8], (N_EVEN, CONV_WIDTH, A_WIDTH), CONV_WIDTH ** -0.5),
        'even_ln_g': 1.0 + nrm(ks[9], (N_EVEN, B_WIDTH), 0.02),
        'even_ln_b': nrm(ks[10], (N_EVEN, B_WIDTH), 0.02),
        'even_w_s': nrm(ks[11], (N_EVEN, B_GROUPS, B_CHUNK, B_CHUNK), B_CHUNK ** -0.5),
        'even_b_s': nrm(ks[12], (N_EVEN, B_CHUNK, B_GROUPS), 0.1),
        'even_w_out': nrm(ks[13], (N_EVEN, EVEN_MIX, D_MODEL), EVEN_MIX ** -0.5),
        'odd_w_in': nrm(ks[14], (N_ODD, D_MODEL, ODD_IN), D_MODEL ** -0.5),
        'odd_b_if': b_if,
        'odd_mh_g': 1.0 + nrm(ks[15], (N_ODD, C_HEADS, C_DV), 0.02),
        'odd_w_out': nrm(ks[18], (N_ODD, C_WIDTH, D_MODEL), C_WIDTH ** -0.5),
    }

def reference(x, p, pre_g, post_g, ple_g, w_ple, w_ple_gate, even_w_in, even_conv_w, even_ln_g,
              even_ln_b, even_w_s, even_b_s, even_w_out, odd_w_in, odd_b_if, odd_mh_g, odd_w_out):
    h = x
    for i in range(DEPTH):
        j = i // 2
        xn = rmsnorm(h, pre_g[i])
        if i % 2 == 0:
            y = conv_gmlp_mixer(xn, even_w_in[j], even_conv_w[j], even_ln_g[j], even_ln_b[j],
                                even_w_s[j], even_b_s[j], even_w_out[j])
        else:
            y = mlstm_mixer(xn, odd_w_in[j], odd_b_if[j], odd_mh_g[j], odd_w_out[j])
        h = h + rmsnorm(y, post_g[i])
        gate = jax.nn.sigmoid(rmsnorm(h, ple_g[i]) @ w_ple_gate[i])
        h = h + gate * (p[i] @ w_ple[i])
    return h


_drawn_inputs = setup_inputs


def setup_inputs(seed=0):
    import zlib

    import numpy as np

    out = dict(_drawn_inputs(seed))
    spreads = {}
    factors = {'ple_g': 28.867, 'even_ln_g': 15.351, 'even_ln_b': 15.567, 'odd_mh_g': 26.342}
    for name, (base, spread) in spreads.items():
        noise = np.random.default_rng([zlib.crc32(name.encode()), seed]).standard_normal(out[name].shape)
        drawn = base * np.exp(spread * noise) if base else spread * noise
        out[name] = __import__('jax').numpy.asarray(drawn.astype(out[name].dtype))
    for name, factor in factors.items():
        out[name] = (out[name] * factor).astype(out[name].dtype)
    return out
```

```python
import concourse.bass as bass
from concourse import mybir

F32 = mybir.dt.float32
F32R = mybir.dt.float32r
ACT = mybir.ActivationFunctionType
ALU = mybir.AluOpType

P = 128
SEQ = 512
D = 1024
TILES = SEQ // P
KD = D // P
PLE = 256
WIDE = 2048
HEADS = 8
DV = 256
EPS = 1e-6
SLOT = 2048
NEVER = -1e30

S_EV = 0
S_EA = S_EV + 4
S_EB = S_EA + 16
S_OUT = [S_EB + 8, 0]
S_PLE = [S_OUT[0] + 8, 0]
S_GATE = [S_PLE[0] + 1, 0]
S_OV0 = S_GATE[0] + 4
S_GIF = S_OV0 + 2
S_QK0 = S_GIF + 1
S_PAIR = S_QK0 + 2
S_OUT[1] = S_PAIR + 3 * 8 + 4
S_PLE[1] = S_OUT[1] + 8
S_GATE[1] = S_PLE[1] + 1
SLOTS = S_GATE[1] + 4

N_EV = 0
N_EA = N_EV + 8
N_EB = N_EA + 32
N_OUT = [N_EB + 16, 0]
N_PLE = [N_OUT[0] + 8, 0]
N_GATE = [N_PLE[0] + 8, 0]
N_OV0 = N_GATE[0] + 8
N_GIF = N_OV0 + 4
N_QK0 = N_GIF + 1
N_PAIR = N_QK0 + 4
N_OUT[1] = N_PAIR + 3 * 16 + 8
N_PLE[1] = N_OUT[1] + 8
N_GATE[1] = N_PLE[1] + 8



def slot_ends():
    ends, halves = [], 0

    def half():
        nonlocal halves
        halves += 1
        ends.append((HALF, halves))

    def full(n):
        ends.append((PRODUCT, n))

    def tail(l):
        for nb in range(2):
            for _ in range(3):
                half()
            full(N_OUT[l] + 4 * nb + 4)
        full(N_PLE[l] + 8)
        for nb in range(2):
            half()
            full(N_GATE[l] + 4 * nb + 4)

    for nb in range(2):
        half()
        full(N_EV + 4 * nb + 4)
    for n in range(16):
        full(N_EA + 2 * n + 2)
    for n in range(8):
        full(N_EB + 2 * n + 2)
    tail(0)
    half()
    full(N_OV0 + 4)
    full(N_GIF + 1)
    full(N_QK0 + 2)
    full(N_QK0 + 4)
    for j in range(4):
        for k in range(4):
            full(N_PAIR + 16 * j + 2 * k + 2)
        if j < 3:
            half()
            full(N_PAIR + 16 * j + 12)
            full(N_PAIR + 16 * j + 14)
            full(N_PAIR + 16 * j + 16)
    tail(1)
    return ends


HALF, PRODUCT = range(2)
SLOT_END = slot_ends()
assert len(SLOT_END) == SLOTS

A_EV = 0
A_EA = 8
A_PLE = [16, 0]
A_GATE = [24, 0]
A_OV0 = 32
A_QK0 = 36
A_PAIR = 40
A_PLE[1] = A_PAIR + 3 * 12 + 4
A_GATE[1] = A_PLE[1] + 8

V_EA = 0
V_EB = 24
V_OUT = [40, 0]
V_GIF = 48
V_PAIR = 49
V_OUT[1] = V_PAIR + 16


def trunk(nc, x, p_in, slots, g_rows, ln_rows, w_mix, b_mix, conv_w, gate_bias, head_g, out):
    base = (nc.sbuf_base + 63) // 64 * 64
    place = [base]

    def fixed(name, shape, dtype=F32):
        size = 4
        for n in shape[1:]:
            size *= n
        t = nc.alloc_sbuf_tensor_at(name, shape, dtype, offset=place[0])
        place[0] += (size + 31) // 32 * 32
        return t

    raw = fixed("raw", [P, 2, SLOT])
    w_hi = fixed("w_hi", [P, 2, SLOT], F32R)
    w_lo = fixed("w_lo", [P, 2, SLOT], F32R)
    x_hi = fixed("x_hi", [P, KD, SEQ], F32R)
    x_lo = fixed("x_lo", [P, KD, SEQ], F32R)
    y_hi_at = place[0]
    y_hi = fixed("y_hi", [P, 16, SEQ], F32R)
    y_lo_at = place[0]
    y_lo = fixed("y_lo", [P, 16, SEQ], F32R)
    h = fixed("h", [P, TILES, D])
    ident = fixed("ident", [P, P])
    scaled = fixed("scaled", [P, 2, D])
    g_pre = fixed("g_pre", [P, D])
    square = fixed("square", [P, D])
    sums = fixed("sums", [P, 64])
    rstds = fixed("rstds", [P, 64])
    conv_sb = fixed("conv_sb", [P, 3, 8])
    head_g_sb = fixed("head_g_sb", [P, 16])
    bias_sb = fixed("bias_sb", [P, 1])
    minus_half = fixed("minus_half", [P, 8])
    eps_tile = fixed("eps_tile", [P, 8])
    shared_at = place[0]

    def staged(spec, at):
        made = []
        for name, shape, dtype in spec:
            size = 4
            for n in shape[1:]:
                size *= n
            made.append(nc.alloc_sbuf_tensor_at(name, shape, dtype, offset=at))
            at += (size + 31) // 32 * 32
        assert at <= nc.sbuf_usable_end, at
        return made

    ln_g, ln_b, wt, bt, act_t, conv_in, silu_t, acc, bn_out, bn_mv = staged([
        ("ln_g", [P, D], F32), ("ln_b", [P, D], F32), ("wt", [P, 8, P], F32), ("bt", [P, 8, P], F32),
        ("act_t", [P, 2, SEQ], F32), ("conv_in", [P, 2, SEQ + 2], F32), ("silu_t", [P, 2, SEQ], F32),
        ("acc", [P, 2, SEQ], F32), ("bn_out", [P, TILES, 2, 6], F32), ("bn_mv", [P, TILES, 2], F32)], shared_at)
    v_even, = staged([("v_even", [P, 8, TILES, P], F32)], y_hi_at + 8 * SEQ * 4)
    p_hi, p_lo, p_sb, g_post, g_ple, tanh_g, gated = staged([
        ("p_hi", [P, 2, SEQ], F32R), ("p_lo", [P, 2, SEQ], F32R), ("p_sb", [P, TILES, PLE], F32),
        ("g_post", [P, D], F32), ("g_ple", [P, D], F32), ("tanh_g", [P, 2, SEQ], F32),
        ("gated", [P, 2, SEQ], F32)], shared_at)
    ple, = staged([("ple", [P, TILES, D], F32)], y_lo_at)
    (v_odd, gates, expo, q_in, kw, state, num, r_hi, r_lo, rm_hi, rm_lo, ones8, sc, mask,
     den, rcp, rcp2, msq, fac, ssn) = staged([
        ("v_odd", [P, TILES, 2, DV + 1], F32), ("gates", [P, 4, SEQ], F32), ("expo", [P, SEQ], F32), ("q_in", [P, 3, P], F32),
        ("kw", [P, 3, P], F32), ("state", [P, 3, DV + 1], F32), ("num", [P, 2, TILES, DV + 1], F32),
        ("r_hi", [8, SEQ], F32R), ("r_lo", [8, SEQ], F32R), ("rm_hi", [8, SEQ], F32R),
        ("rm_lo", [8, SEQ], F32R), ("ones8", [8, P], F32R), ("sc", [P, 4, TILES, HEADS], F32), ("mask", [P, P], F32),
        ("den", [P, 2, 4], F32), ("rcp", [P, 2, 4], F32), ("rcp2", [P, 2, 4], F32), ("msq", [P, 2, 4], F32),
        ("fac", [P, 2, 4], F32), ("ssn", [P, 2, 4], F32)], shared_at)
    tanh_o = g_pre[:, :].rearrange("p (f t) -> p f t", f=2)
    tanh_z = scaled[:, 0].rearrange("p (f t) -> p f t", f=2)
    yy = scaled[:, 1].rearrange("p (f t) -> p f t", f=2)
    qk, = staged([("qk", [P, 4, SEQ], F32)], y_lo_at + 12 * SEQ * 4)
    isc = square[:, 0:3 * P].rearrange("p (n t) -> p n t", n=3)
    rows, = staged([("rows", [8, 8, SEQ], F32)], y_hi_at)
    R_I, R_F, R_T, R_B, R_C, R_M, R_X, R_ONE = range(8)
    tok_rows, m_prev, decay8, diag = staged([
        ("tok_rows", [8, 3, SEQ], F32), ("m_prev", [8, 8], F32), ("decay8", [8, 4], F32),
        ("diag", [8, 2, 8], F32)], y_lo_at)
    SC_C, SC_E, SC_W, SC_D = range(4)
    bank = [nc.alloc_psum_tensor(f"bank{b}", [P, SEQ], F32) for b in range(8)]

    sem = nc.alloc_semaphore
    raw_in = [sem("raw_in0"), sem("raw_in1")]
    x_in = [sem(f"x_in{t}") for t in range(TILES)]
    g_in = sem("g_in")
    const_in = sem("const_in")
    tail_in = sem("tail_in")
    stored = sem("stored")
    hi_ready = sem("hi_ready")
    lo_ready = sem("lo_ready")
    half_used = sem("half_used")
    product_ready = sem("product_ready")
    act_freed = sem("act_freed")
    dve_freed = sem("dve_freed")
    ident_ready = sem("ident_ready")
    const_ready = sem("const_ready")
    pre_sum = sem("pre_sum")
    post_sum = sem("post_sum")
    pool_step = sem("pool_step")
    pre_rstd = sem("pre_rstd")
    post_rstd = sem("post_rstd")
    ln_rstd = sem("ln_rstd")
    head_rstd = sem("head_rstd")
    scaled_ready = sem("scaled_ready")
    xt_ready = sem("xt_ready")
    xhi_ready = sem("xhi_ready")
    xlo_ready = sem("xlo_ready")
    pt_ready = sem("pt_ready")
    phi_ready = sem("phi_ready")
    plo_ready = sem("plo_ready")
    h_ready = sem("h_ready")
    gated_ready = sem("gated_ready")
    silu_in = sem("silu_in")
    ln_stats = sem("ln_stats")
    vst_ready = sem("vst_ready")
    mix_ready = sem("mix_ready")
    wt_ready = sem("wt_ready")
    y_ready = sem("y_ready")
    dve_step = sem("dve_step")
    act_step = sem("act_step")
    gif_ready = sem("gif_ready")
    gif_act = sem("gif_act")
    rows_ready = sem("rows_ready")
    rowst_ready = sem("rowst_ready")
    sc_ready = sem("sc_ready")
    rm_ready = sem("rm_ready")
    scores_ready = sem("scores_ready")
    isc_ready = sem("isc_ready")
    arg_ready = sem("arg_ready")
    exp_ready = sem("exp_ready")
    kw_ready = sem("kw_ready")
    probs_ready = sem("probs_ready")
    dstate_ready = sem("dstate_ready")
    state_ready = sem("state_ready")
    num_ready = sem("num_ready")
    num_used = sem("num_used")
    msq_ready = sem("msq_ready")
    hc_ready = sem("hc_ready")
    yt_ready = sem("yt_ready")

    def wait_slot_used(eng, s, i, per_step):
        kind, value = SLOT_END[s]
        stride = 0
        if per_step:
            kind2, value2 = SLOT_END[s + per_step]
            assert kind2 == kind
            stride = value2 - value
        eng.wait_ge(half_used if kind == HALF else product_ready, stride * i + value)

    block = nc.Block()
    block.__enter__()

    @block.sync
    def _(sp):
        def load(s, r, wait=True):
            if wait:
                sp.wait_ge(lo_ready, 2 * s - 2)
            sp.dma_start(raw[:, r], slots[s] if isinstance(s, int) else
                         slots[bass.ds(s, 1)].rearrange("a p n -> (a p) n")).then_inc(raw_in[r], 16)

        def row(dst, src, done):
            sp.dma_start(dst[:, :], src.to_broadcast([P, D])).then_inc(done, 16)

        sp.dma_start(h[:, 0], x[0:P, :]).then_inc(x_in[0], 16)
        row(g_pre, g_rows[0:1, :], g_in)
        sp.dma_start(h[:, 1], x[P:2 * P, :]).then_inc(x_in[1], 16)
        load(0, 0, wait=False)
        for t in range(2, TILES):
            sp.dma_start(h[:, t], x[t * P:(t + 1) * P, :]).then_inc(x_in[t], 16)
        load(1, 1, wait=False)
        row(ln_g, ln_rows[0:1, :], const_in)
        row(ln_b, ln_rows[1:2, :], const_in)
        sp.dma_start(wt[:, :, :], w_mix).then_inc(const_in, 16)
        sp.dma_start(bt[:, :, :].rearrange("p g t -> p (g t)"), b_mix.to_broadcast([P, 8 * P])).then_inc(const_in, 16)
        sp.dma_start(conv_sb[:, :, :], conv_w).then_inc(const_in, 16)
        sp.dma_start(head_g_sb[:, :], head_g).then_inc(const_in, 16)
        sp.dma_start(bias_sb[0:8, :], gate_bias[0:8, :]).then_inc(const_in, 16)
        sp.dma_start(bias_sb[32:40, :], gate_bias[8:16, :]).then_inc(const_in, 16)

        def loads(first, last):
            steps = (last - first) // 2
            with sp.Fori(0, steps) as i:
                for r in range(2):
                    load(2 * i + (first + r), (first + r) % 2)
            for s in range(first + 2 * steps, last):
                load(s, s % 2)

        def tail(l):
            sp.wait_ge(y_ready, 16 * (l + 1))
            sp.dma_start(p_sb[:, :, :], p_in[l].rearrange("(t q) c -> q t c", q=P)).then_inc(tail_in, 16)
            row(g_post, g_rows[3 * l + 1:3 * l + 2, :], tail_in)
            row(g_ple, g_rows[3 * l + 2:3 * l + 3, :], tail_in)
            if l == 0:
                row(g_pre, g_rows[3:4, :], tail_in)

        loads(2, S_OUT[0] + 3)
        tail(0)
        loads(S_OUT[0] + 3, S_OUT[1] + 4)
        tail(1)
        loads(S_OUT[1] + 4, SLOTS)
        for half in range(2):
            c = slice(half * SEQ, (half + 1) * SEQ)
            for t in range(TILES):
                sp.wait_ge(gated_ready, 8 + (4 * half + t) + 1)
                sp.dma_start(out[t * P:(t + 1) * P, c], h[:, t, c]).then_inc(stored, 16)
        sp.wait_ge(stored, 16 * 2 * TILES)

    @block.gpsimd
    def _(pool):
        steps = [0]

        def link(ins):
            ins.then_inc(pool_step, 1)
            steps[0] += 1
            pool.wait_ge(pool_step, steps[0])

        link(pool.memset(ident[:, :], 0.0))
        pool.affine_select(out=ident[:, :], in_=ident[:, :], compare_op=ALU.not_equal, fill=1.0, base=0,
                           pattern=[[-1, P]], channel_multiplier=1).then_inc(ident_ready, 1)
        pool.memset(minus_half[:, :], -0.5).then_inc(const_ready, 1)
        pool.memset(eps_tile[:, :], EPS).then_inc(const_ready, 1)
        pool.wait_ge(const_ready, 2)

        def rstd_of(ready, count, first, second, dst, done):
            pool.wait_ge(ready, count)
            link(pool.tensor_tensor(dst, first, second, ALU.add))
            link(pool.tensor_scalar(dst, dst, 1.0 / D, EPS, ALU.mult, ALU.add))
            pool.tensor_tensor(dst, dst, minus_half[:, 0:1], ALU.pow).then_inc(done, 1)

        def pre(e):
            count = 2 * e + 2 if e // 4 != 2 else 20 + e - 8 + 1
            rstd_of(pre_sum, count, sums[:, 2 * e:2 * e + 1], sums[:, 2 * e + 1:2 * e + 2],
                    rstds[:, e:e + 1], pre_rstd)

        def post(l, t):
            c = 32 + 8 * l + 2 * t
            rstd_of(post_sum, 8 * l + 4 + t + 1, sums[:, c:c + 1], sums[:, c + 1:c + 2],
                    rstds[:, 16 + 4 * l + t:17 + 4 * l + t], post_rstd)

        for t in range(TILES):
            pre(t)
        pool.wait_ge(const_in, 16 * 8)
        pool.affine_select(out=wt[:, :, :], in_=wt[:, :, :], compare_op=ALU.is_ge, fill=0.0, base=0,
                           pattern=[[0, 8], [1, P]], channel_multiplier=-1).then_inc(wt_ready, 1)
        for t in range(TILES):
            pool.wait_ge(ln_stats, t + 1)
            link(pool.tensor_scalar(rstds[:, 32 + t:33 + t], bn_mv[:, t, 1:2], 1.0, EPS, ALU.mult, ALU.add))
            pool.tensor_tensor(rstds[:, 32 + t:33 + t], rstds[:, 32 + t:33 + t], minus_half[:, 0:1],
                               ALU.pow).then_inc(ln_rstd, 1)

        def tail_norms(l):
            e = 4 + 8 * l
            post(l, 0)
            post(l, 1)
            pre(e)
            post(l, 2)
            pre(e + 1)
            post(l, 3)
            pre(e + 2)
            pre(e + 3)

        tail_norms(0)
        for t in range(TILES):
            pre(8 + t)
        pool.wait_ge(gated_ready, 8)
        link(pool.memset(mask[:, :], 0.0))
        pool.affine_select(out=mask[:, :], in_=mask[:, :], compare_op=ALU.is_ge, fill=NEVER, base=0,
                           pattern=[[1, P]], channel_multiplier=-1).then_inc(wt_ready, 1)
        fixed_steps = steps[0]
        with pool.Fori(0, HEADS // 2) as j:
            for a in range(2):
                pool.wait_ge(msq_ready, 2 * j + (a + 1))
                pool.tensor_tensor(msq[:, a], msq[:, a], eps_tile[:, 0:4], ALU.add).then_inc(pool_step, 1)
                pool.wait_ge(pool_step, 2 * j + (fixed_steps + a + 1))
                pool.tensor_tensor(msq[:, a], msq[:, a], minus_half[:, 0:4], ALU.pow).then_inc(head_rstd, 1)
        steps[0] += HEADS
        tail_norms(1)

    @block.scalar
    def _(act):
        def hi(s, i=0, per_step=0):
            r = s % 2
            act.wait_ge(raw_in[r], 8 * per_step * i + (8 * s + 16 - 8 * r))
            if s >= 2:
                wait_slot_used(act, s - 2, i, per_step)
            for half in range(2):
                c = slice(half * SLOT // 2, (half + 1) * SLOT // 2)
                act.activation(w_hi[:, r, c], raw[:, r, c], ACT.Copy).then_inc(hi_ready, 1)

        def h_square(e, t, half):
            square_any(h[:, t, half * SEQ:(half + 1) * SEQ], sums[:, 2 * e + half:2 * e + half + 1], pre_sum)

        last = {}

        def square_any(src, dst, done):
            if last:
                act.wait_ge(last["sem"], last["n"])
            act.activation(square[:, 0:SEQ], src, ACT.Square, accum_out=dst).then_inc(done, 1)
            count[id(done)] = count.get(id(done), 0) + 1
            last.update(sem=done, n=count[id(done)])

        count = {}

        def x_high(e, t):
            for q in range(2):
                act.wait_ge(xt_ready, 2 * e + q + 1)
                act.activation(x_hi[:, 4 * q:4 * q + 4, t * P:(t + 1) * P],
                               bank[norm_bank(e, t) + q][:, :].rearrange("p (k c) -> p k c", k=4),
                               ACT.Copy).then_inc(xhi_ready, 1)

        def x_squares(t):
            act.wait_ge(x_in[t], 16)
            for half in range(2):
                h_square(t, t, half)

        x_squares(0)
        x_squares(1)
        x_high(0, 0)
        hi(0)
        x_squares(2)
        x_high(1, 1)
        x_squares(3)
        x_high(2, 2)
        hi(1)
        x_high(3, 3)

        for s in range(4):
            hi(s + 2)
            if s % 2:
                for t in range(TILES):
                    act.wait_ge(product_ready, N_EV + 4 * (s // 2) + t + 1)
                    act.activation(v_even[:, 4 * (s // 2):4 * (s // 2) + 4, t, :],
                                   bank[4 * (s // 2) + t][:, :].rearrange("p (g c) -> p g c", g=4),
                                   ACT.Copy).then_inc(act_freed, 1)

        def group_a(i):
            first = not isinstance(i, int) or i > 0
            hi(S_EA + 2, i, 4)
            for f in range(2):
                act.wait_ge(product_ready, 8 * i + (N_EA + f + 1))
                if first:
                    act.wait_ge(dve_freed, 6 * i + (V_EA - 4 + f + 1))
                act.activation(act_t[:, f], bank[f][:, :], ACT.Copy).then_inc(act_freed, 1)
            hi(S_EA + 3, i, 4)
            hi(S_EA + 4, i, 4)
            for f in range(2):
                act.wait_ge(product_ready, 8 * i + (N_EA + 4 + f + 1))
                act.wait_ge(dve_freed, 6 * i + (V_EA + f + 1))
                act.activation(act_t[:, f], bank[4 + f][:, :], ACT.Tanh, scale=0.5).then_inc(silu_in, 1)
            hi(S_EA + 5, i, 4)

        group_a(0)
        with act.Fori(1, 4) as i:
            group_a(i)

        with act.Fori(0, 4) as i:
            hi(S_EB + 2, i, 2)
            for f in range(2):
                act.wait_ge(product_ready, 4 * i + (N_EB + f + 1))
                act.wait_ge(dve_freed, 4 * i + (V_EB - 4 + f + 1))
                act.activation(act_t[:, f], bank[f][:, :], ACT.Tanh, scale=0.5).then_inc(silu_in, 1)
            hi(S_EB + 3, i, 2)

        def tail(l):
            s, n = S_OUT[l], N_OUT[l]
            for q in range(4):
                hi(s + q + 2)
            for q in range(2):
                act.wait_ge(pt_ready, 2 * l + q + 1)
                act.activation(p_hi[:, q, :], bank[6 + q][:, :], ACT.Copy).then_inc(phi_ready, 1)
            for t in range(TILES):
                act.wait_ge(product_ready, n + t + 1)
                c = 32 + 8 * l + 2 * t
                square_any(bank[t][:, :], sums[:, c:c + 1], post_sum)
            for q in range(4, 7):
                hi(s + q + 2)

            def y_square(t):
                act.wait_ge(product_ready, n + 4 + t + 1)
                c = 33 + 8 * l + 2 * t
                square_any(bank[4 + t][:, :], sums[:, c:c + 1], post_sum)

            def ple_norm(t):
                act.wait_ge(h_ready, 4 * l + t + 1)
                for half in range(2):
                    h_square(4 + 8 * l + t, t, half)

            def ple_copy(nb, t):
                act.wait_ge(product_ready, N_PLE[l] + PLE_ORDER.index((nb, t)) + 1)
                act.activation(ple[:, t, nb * SEQ:(nb + 1) * SEQ], bank[t][:, :], ACT.Copy).then_inc(act_freed, 1)

            def x_h(t):
                x_high(4 + 8 * l + t, t)

            y_square(0)
            y_square(1)
            ple_norm(0)
            y_square(2)
            ple_norm(1)
            y_square(3)
            ple_copy(0, 0)
            ple_copy(0, 1)
            ple_copy(0, 2)
            x_h(0)
            ple_norm(2)
            hi(S_PLE[l] + 1)
            ple_norm(3)
            ple_copy(1, 0)
            ple_copy(1, 1)
            ple_copy(0, 3)
            x_h(1)
            ple_copy(1, 2)
            x_h(2)
            ple_copy(1, 3)
            hi(S_PLE[l] + 2)
            x_h(3)

            s = S_GATE[l]

            def tanh(nb, t):
                k = 8 * l + 4 * nb + t
                act.wait_ge(product_ready, N_GATE[l] + 4 * nb + t + 1)
                if k >= 2:
                    act.wait_ge(gated_ready, k - 1)
                act.activation(tanh_g[:, k % 2], bank[4 * nb + t][:, :], ACT.Tanh,
                               scale=0.5).then_inc(act_freed, 1)

            def next_norm(t, half):
                if l == 0:
                    act.wait_ge(gated_ready, 4 * half + t + 1)
                    h_square(8 + t, t, half)

            hi(s + 2)
            hi(s + 3)
            for t in range(TILES):
                tanh(0, t)
            for t in range(TILES):
                next_norm(t, 0)
            if l == 0:
                hi(s + 4)
            tanh(1, 0)
            tanh(1, 1)
            next_norm(0, 1)
            tanh(1, 2)
            next_norm(1, 1)
            if l == 0:
                x_high(8, 0)
            tanh(1, 3)
            if l == 0:
                next_norm(2, 1)
                x_high(9, 1)
                next_norm(3, 1)
                x_high(10, 2)
                hi(s + 5)
                x_high(11, 3)

        tail(0)

        def v_copy(j, n0, first_bank, tiles=range(TILES)):
            for t in tiles:
                act.wait_ge(product_ready, 16 * j + (n0 + t + 1))
                act.activation(v_odd[:, t, :, 0:DV], bank[first_bank + t][:, :].rearrange("p (a c) -> p a c", a=2),
                               ACT.Copy).then_inc(act_freed, 1)

        def qk_copy(j, n0, a):
            for c in (2 * a, 2 * a + 1):
                act.wait_ge(product_ready, 16 * j + (n0 + c + 1))
                act.activation(qk[:, c], bank[c][:, :], ACT.Copy,
                               scale=float(P) ** -0.5 if c % 2 == 0 else 1.0).then_inc(act_freed, 1)

        hi(S_OV0 + 2)
        hi(S_OV0 + 3)
        v_copy(0, N_OV0, 4)
        hi(S_GIF + 2)
        act.wait_ge(gif_ready, 1)
        act.activation(rows[:, R_T], rows[:, R_T], ACT.Exp, scale=-1.0).then_inc(gif_act, 1)
        act.wait_ge(gif_act, 1)
        act.activation(rows[:, R_T], rows[:, R_T], ACT.Ln, bias=rows[:, R_ONE, 0:1]).then_inc(gif_act, 1)
        hi(S_QK0 + 2)
        act.wait_ge(gif_ready, 2)
        act.activation(decay8[:, :], rows[:, R_X].rearrange("p (n t) -> p n t", n=4)[:, :, P - 1], ACT.Exp)\
           .then_inc(gif_act, 1)
        qk_copy(0, N_QK0, 0)
        hi(S_QK0 + 3)
        qk_copy(0, N_QK0, 1)
        act.wait_ge(rowst_ready, 1)
        for kind, func in ((SC_C, ACT.Copy), (SC_E, ACT.Exp), (SC_W, ACT.Exp)):
            act.activation(sc[:, kind].rearrange("p n h -> p (n h)"), bank[7][:, 32 * kind:32 * kind + 32],
                           func).then_inc(sc_ready, 1)
        act.activation(sc[:, SC_D, 0:2].rearrange("p n h -> p (n h)"), bank[7][:, 96:112], ACT.Copy)\
           .then_inc(sc_ready, 1)

        def pair(j, more):
            s = 8 * j + S_PAIR

            def rowscale(a):
                act.wait_ge(scores_ready, 6 * j + (3 * a + 1))
                act.activation(isc, bank[4][:, P:SEQ].rearrange("p (n t) -> p n t", n=3), ACT.Exp)\
                   .then_inc(isc_ready, 1)
                act.wait_ge(arg_ready, 2 * j + (a + 1))
                act.activation(expo[:, :], expo[:, :], ACT.Exp).then_inc(exp_ready, 1)

            def o_tanh(a):
                for f in range(2):
                    act.wait_ge(product_ready, 16 * j + (N_PAIR + 4 * a + f + 1))
                    act.activation(tanh_o[:, f], bank[f][:, :], ACT.Tanh, scale=0.5).then_inc(act_freed, 1)

            def z_tanh(a):
                for f in range(2):
                    act.wait_ge(product_ready, 16 * j + (N_PAIR + 4 * a + 2 + f + 1))
                    act.activation(tanh_z[:, f], bank[2 + f][:, :], ACT.Tanh, scale=0.5).then_inc(silu_in, 1)

            def num_copy(a):
                for n, b in enumerate(NUM_BANK):
                    k = 4 * a + n
                    act.wait_ge(num_ready, 8 * j + (k + 1))
                    act.activation(num[:, a, n, :], bank[b][:, 0:DV + 1], ACT.Copy).then_inc(act_step, 1)
                    if k:
                        act.wait_ge(num_used, 8 * j + k)
                    act.activation(square[:, SEQ:SEQ + DV], bank[b][:, 0:DV], ACT.Square,
                                   accum_out=ssn[:, a, n:n + 1]).then_inc(num_used, 1)

            rowscale(0)
            hi(S_PAIR + 2, j, 8)
            o_tanh(0)
            hi(S_PAIR + 3, j, 8)
            z_tanh(0)
            num_copy(0)
            rowscale(1)
            hi(S_PAIR + 4, j, 8)
            o_tanh(1)
            hi(S_PAIR + 5, j, 8)
            z_tanh(1)
            num_copy(1)
            if more:
                hi(S_PAIR + 6, j, 8)
                v_copy(j, N_PAIR + 8, 0, (0, 1))
                hi(S_PAIR + 7, j, 8)
                v_copy(j, N_PAIR + 8, 0, (2, 3))
                qk_copy(j, N_PAIR + 12, 0)
                hi(S_PAIR + 8, j, 8)
                qk_copy(j, N_PAIR + 12, 1)
                hi(S_PAIR + 9, j, 8)

        assert S_PAIR % 2 == 0
        act.wait_ge(pre_sum, 24)
        with act.Fori(0, 3) as j:
            pair(j, True)
        pair(3, False)
        act.wait_ge(probs_ready, HEADS)
        tail(1)

    @block.vector
    def _(dve):
        def lo(s, i=0, per_step=0):
            r = s % 2
            if s >= 2:
                wait_slot_used(dve, s - 2, i, per_step)
            for half in range(2):
                c = slice(half * SLOT // 2, (half + 1) * SLOT // 2)
                dve.wait_ge(hi_ready, 2 * per_step * i + (2 * s + half + 1))
                dve.tensor_tensor(w_lo[:, r, c], raw[:, r, c], w_hi[:, r, c].bitcast(F32),
                                  ALU.subtract).then_inc(lo_ready, 1)

        own = {"n": 0, "i": 0, "stride": 0}

        def step(ins):
            ins.then_inc(dve_step, 1)
            own["n"] += 1
            dve.wait_ge(dve_step, own["i"] * own["stride"] + own["n"])

        def enter(i, stride):
            own.update(i=i, stride=stride, start=own["n"])

        def leave(passes):
            assert own["n"] - own["start"] == own["stride"], own
            own.update(i=0, n=own["start"] + passes * own["stride"], stride=0)

        def normalise(e, t, g):
            dve.wait_ge(pre_rstd, e + 1)
            if e % 4 >= 2:
                dve.wait_ge(xt_ready, 2 * e - 2)
            dve.scalar_tensor_tensor(scaled[:, t % 2], h[:, t], rstds[:, e:e + 1], g[:, :], ALU.mult,
                                     ALU.mult).then_inc(scaled_ready, 1)

        def x_low(e, t):
            for q in range(2):
                dve.wait_ge(xhi_ready, 2 * e + q + 1)
                at = (slice(None), slice(4 * q, 4 * q + 4), slice(t * P, (t + 1) * P))
                dve.tensor_tensor(x_lo[at], bank[norm_bank(e, t) + q][:, :].rearrange("p (k c) -> p k c", k=4),
                                  x_hi[at].bitcast(F32), ALU.subtract).then_inc(xlo_ready, 1)

        dve.wait_ge(g_in, 16)
        normalise(0, 0, g_pre)
        normalise(1, 1, g_pre)
        x_low(0, 0)
        lo(0)
        normalise(2, 2, g_pre)
        x_low(1, 1)
        normalise(3, 3, g_pre)
        x_low(2, 2)
        lo(1)
        x_low(3, 3)

        dve.memset(conv_in[:, :, 0:2], 0.0).then_inc(dve_step, 1)
        own["n"] += 1
        dve.wait_ge(const_in, 16 * 8)
        step(dve.tensor_scalar(conv_sb[:, :, :], conv_sb[:, :, :], 0.5, None, ALU.mult))
        step(dve.tensor_scalar(head_g_sb[:, :], head_g_sb[:, :], 0.25, None, ALU.mult))
        for s in range(4):
            lo(s + 2)
            if s % 2:
                for t in range(TILES):
                    dve.wait_ge(act_freed, A_EV + 4 * (s // 2) + t + 1)
                    dve.bn_stats(bn_out[:, t, s // 2], v_even[:, 4 * (s // 2):4 * (s // 2) + 4, t, :])\
                       .then_inc(dve_step, 1)
                    own["n"] += 1
        dve.wait_ge(dve_step, own["n"])
        for t in range(TILES):
            dve.bn_aggr(bn_mv[:, t], bn_out[:, t]).then_inc(ln_stats, 1)
        for t in range(TILES):
            dve.wait_ge(ln_rstd, t + 1)
            dve.tensor_scalar(v_even[:, :, t, :], v_even[:, :, t, :], bn_mv[:, t, 0:1], rstds[:, 32 + t:33 + t],
                              ALU.subtract, ALU.mult).then_inc(dve_step, 1)
            own["n"] += 1
        dve.wait_ge(dve_step, own["n"])

        def split_y(f, tile, src):
            at = bass.ds(tile, 1)
            step(dve.tensor_scalar(y_hi[:, at, :].rearrange("p a t -> p (a t)"), src, 1.0, None, ALU.mult))
            dve.tensor_tensor(y_lo[:, at, :].rearrange("p a t -> p (a t)"), src,
                              y_hi[:, at, :].rearrange("p a t -> p (a t)").bitcast(F32),
                              ALU.subtract).then_inc(y_ready, 1)

        def group_a(i):
            lo(S_EA + 2, i, 4)
            lo(S_EA + 3, i, 4)
            for f in range(2):
                dve.wait_ge(product_ready, 8 * i + (N_EA + 2 + f + 1))
                dve.wait_ge(act_freed, 2 * i + (A_EA + f + 1))
                dve.tensor_tensor(conv_in[:, f, 2:], bank[2 + f][:, :], act_t[:, f], ALU.mult)\
                   .then_inc(dve_freed, 1)
            for f in range(2):
                dve.wait_ge(dve_freed, 6 * i + (V_EA + f + 1))
                if f == 0 and not (isinstance(i, int) and i == 0):
                    dve.wait_ge(y_ready, 2 * i)
                for tap in (2, 1, 0):
                    w = conv_sb[:, tap, bass.ds(2 * i + f, 1)]
                    if tap == 2:
                        step(dve.tensor_scalar(acc[:, f], conv_in[:, f, 2:SEQ + 2], w, None, ALU.mult))
                    else:
                        step(dve.scalar_tensor_tensor(acc[:, f], conv_in[:, f, tap:tap + SEQ], w, acc[:, f],
                                                      ALU.mult, ALU.add))
            lo(S_EA + 4, i, 4)
            for f in range(2):
                dve.wait_ge(silu_in, 2 * i + (f + 1))
                dve.scalar_tensor_tensor(silu_t[:, f], act_t[:, f], 1.0, bank[4 + f][:, :], ALU.add,
                                         ALU.mult).then_inc(dve_freed, 1)
            lo(S_EA + 5, i, 4)
            for f in range(2):
                dve.wait_ge(product_ready, 8 * i + (N_EA + 6 + f + 1))
                dve.tensor_tensor(acc[:, f], acc[:, f], bank[6 + f][:, :], ALU.mult).then_inc(dve_freed, 1)
                dve.wait_ge(dve_freed, 6 * i + (V_EA + 4 + f + 1))
                step(dve.tensor_tensor(acc[:, f], acc[:, f], silu_t[:, f], ALU.mult))
                split_y(f, 2 * i + f, acc[:, f])

        enter(0, 10)
        group_a(0)
        leave(1)
        with dve.Fori(1, 4) as i:
            enter(i - 1, 10)
            group_a(i)
            leave(3)

        def v_group(i):
            for f in range(2):
                dst = conv_in[:, f, 0:SEQ].rearrange("p (n c) -> p n c", n=TILES)
                cols = bass.ds(i * 2 * P + f * P, P)

                def over_tiles(row):
                    return row[:, cols].rearrange("p (a c) -> p a c", a=1).to_broadcast([P, TILES, P])

                step(dve.tensor_tensor(dst, v_even[:, bass.ds(2 * i + f, 1)].rearrange("p a n c -> p (a n) c"),
                                       over_tiles(ln_g), ALU.mult))
                dve.tensor_tensor(dst, dst, over_tiles(ln_b), ALU.add).then_inc(vst_ready, 1)

        def group_b(i, more):
            lo(S_EB + 2, i, 2)
            for f in range(2):
                dve.wait_ge(silu_in, 2 * i + (8 + f + 1))
                dve.scalar_tensor_tensor(silu_t[:, f], act_t[:, f], 1.0, bank[f][:, :], ALU.add,
                                         ALU.mult).then_inc(dve_freed, 1)
            for f in range(2):
                dve.wait_ge(mix_ready, 2 * i + (f + 1))
                step(dve.tensor_tensor(acc[:, f].rearrange("p (n t) -> p n t", n=TILES),
                                       bank[4 + f][:, :].rearrange("p (n t) -> p n t", n=TILES),
                                       bt[:, bass.ds(2 * i + f, 1)].to_broadcast([P, TILES, P]), ALU.add))
            if more:
                v_group(i + 1)
            lo(S_EB + 3, i, 2)
            for f in range(2):
                dve.wait_ge(product_ready, 4 * i + (N_EB + 2 + f + 1))
                dve.tensor_tensor(acc[:, f], acc[:, f], bank[2 + f][:, :], ALU.mult).then_inc(dve_freed, 1)
                dve.wait_ge(dve_freed, 4 * i + (V_EB + 2 + f + 1))
                step(dve.scalar_tensor_tensor(acc[:, f], acc[:, f], 0.5, silu_t[:, f], ALU.mult, ALU.mult))
                split_y(f, 2 * i + (8 + f), acc[:, f])

        v_group(0)
        with dve.Fori(0, 3) as i:
            enter(i, 8)
            group_b(i, True)
            leave(3)
        group_b(3, False)

        def tail(l):
            s = S_OUT[l]
            for q in range(4):
                lo(s + q + 2)
                if l == 1:
                    odd_tail(q)
            for q in range(2):
                dve.wait_ge(phi_ready, 2 * l + q + 1)
                dve.tensor_tensor(p_lo[:, q, :], bank[6 + q][:, :], p_hi[:, q, :].bitcast(F32),
                                  ALU.subtract).then_inc(plo_ready, 1)
            for q in range(4, 7):
                lo(s + q + 2)
            if l == 0:
                dve.wait_ge(tail_in, 16 * 4)
            else:
                dve.wait_ge(tail_in, 16 * 7)

            def residual(t):
                dve.wait_ge(post_rstd, 4 * l + t + 1)
                for nb in range(2):
                    c = slice(nb * SEQ, (nb + 1) * SEQ)
                    dve.scalar_tensor_tensor(term[:, c], bank[4 * nb + t][:, :],
                                             rstds[:, 16 + 4 * l + t:17 + 4 * l + t], g_post[:, c], ALU.mult,
                                             ALU.mult).then_inc(dve_freed, 1)
                dve.wait_ge(dve_freed, V_OUT[l] + 2 * t + 2)
                dve.tensor_tensor(h[:, t], h[:, t], term, ALU.add).then_inc(h_ready, 1)
                dve.wait_ge(h_ready, 4 * l + t + 1)

            term = gated[:, :, :].rearrange("p a c -> p (a c)")
            e = 4 + 8 * l
            residual(0)
            residual(1)
            normalise(e, 0, g_ple)
            residual(2)
            normalise(e + 1, 1, g_ple)
            residual(3)
            x_low(e, 0)
            normalise(e + 2, 2, g_ple)
            lo(S_PLE[l] + 1)
            normalise(e + 3, 3, g_ple)
            x_low(e + 1, 1)
            x_low(e + 2, 2)
            lo(S_PLE[l] + 2)
            x_low(e + 3, 3)

            s = S_GATE[l]

            def gate(nb, t):
                k = 8 * l + 4 * nb + t
                c = slice(nb * SEQ, (nb + 1) * SEQ)
                dve.wait_ge(act_freed, A_GATE[l] + 4 * nb + t + 1)
                step(dve.scalar_tensor_tensor(gated[:, k % 2], tanh_g[:, k % 2], 1.0, ple[:, t, c], ALU.add,
                                              ALU.mult))
                dve.scalar_tensor_tensor(h[:, t, c], gated[:, k % 2], 0.5, h[:, t, c], ALU.mult,
                                         ALU.add).then_inc(gated_ready, 1)
                dve.wait_ge(gated_ready, k + 1)

            lo(s + 2)
            lo(s + 3)
            for t in range(TILES):
                gate(0, t)
            if l == 1:
                for t in range(TILES):
                    gate(1, t)
                return
            lo(s + 4)
            gate(1, 0)
            gate(1, 1)
            normalise(8, 0, g_pre)
            gate(1, 2)
            normalise(9, 1, g_pre)
            x_low(8, 0)
            gate(1, 3)
            normalise(10, 2, g_pre)
            x_low(9, 1)
            normalise(11, 3, g_pre)
            x_low(10, 2)
            lo(s + 5)
            x_low(11, 3)

        def transposed_y(tile, a, f):
            step(dve.scalar_tensor_tensor(yy[:, f], bank[4 + 2 * a + f][:, :], head_g_sb[:, bass.ds(tile, 1)],
                                          gates[:, 2 * a + f], ALU.mult, ALU.mult))
            split_y(f, tile, yy[:, f])

        def odd_tail(q):
            if q in (0, 1):
                for f in range(2):
                    dve.wait_ge(yt_ready, 2 * (6 + q) + f + 1)
                    transposed_y(12 + 2 * q + f, q, f)

        tail(0)

        dve.memset(v_odd[:, :, :, DV:DV + 1], 1.0).then_inc(dve_step, 1)
        own["n"] += 1
        step(dve.memset(rows[:, R_ONE], 1.0))
        step(dve.tensor_copy(ones8[:, :], rows[:, R_ONE, 0:P]))
        lo(S_OV0 + 2)
        lo(S_OV0 + 3)
        dve.wait_ge(product_ready, N_GIF + 1)
        step(dve.tensor_scalar(rows[:, R_I], bank[2][0:8, :], bias_sb[0:8, :], None, ALU.add))
        dve.tensor_scalar(rows[:, R_F], bank[2][32:40, :], bias_sb[32:40, :], None, ALU.add)\
           .then_inc(dve_freed, 1)
        dve.wait_ge(dve_freed, V_GIF + 1)
        dve.scalar_tensor_tensor(rows[:, R_T], rows[:, R_F], -1.0, rows[:, R_F], ALU.mult, ALU.max).then_inc(gif_ready, 1)
        lo(S_GIF + 2)
        step(dve.tensor_scalar(rows[:, R_F], rows[:, R_F], 0.0, None, ALU.min))
        dve.wait_ge(gif_act, 2)
        step(dve.tensor_tensor(rows[:, R_F], rows[:, R_F], rows[:, R_T], ALU.subtract))
        chunk = [slice(n * P, (n + 1) * P) for n in range(TILES)]
        for n in range(TILES):
            step(dve.tensor_tensor_scan(rows[:, R_B, chunk[n]], rows[:, R_ONE, chunk[n]], rows[:, R_F, chunk[n]],
                                        0.0, ALU.mult, ALU.add))
        step(dve.tensor_tensor(rows[:, R_C], rows[:, R_I], rows[:, R_B], ALU.subtract))
        step(dve.memset(m_prev[:, :], 0.0))
        for n in range(TILES):
            end = n * P + P - 1
            step(dve.tensor_tensor_scan(rows[:, R_M, chunk[n]], rows[:, R_C, chunk[n]], rows[:, R_C, chunk[n]],
                                        m_prev[:, n:n + 1], ALU.max, ALU.max))
            step(dve.tensor_tensor(m_prev[:, n + 1:n + 2], rows[:, R_M, end:end + 1], rows[:, R_B, end:end + 1],
                                   ALU.add))
            step(dve.tensor_scalar(rows[:, R_X, chunk[n]], rows[:, R_M, chunk[n]], -1.0, m_prev[:, n:n + 1],
                                   ALU.mult, ALU.add))
            step(dve.tensor_scalar(tok_rows[:, SC_C, chunk[n]], rows[:, R_C, chunk[n]], m_prev[:, n:n + 1], None,
                                   ALU.subtract))
            step(dve.tensor_scalar(tok_rows[:, SC_W, chunk[n]], rows[:, R_C, chunk[n]], rows[:, R_M, end:end + 1],
                                   None, ALU.subtract))
        dve.scalar_tensor_tensor(tok_rows[:, SC_E], rows[:, R_B], -1.0, rows[:, R_M], ALU.mult,
                                 ALU.subtract).then_inc(gif_ready, 1)
        step(dve.tensor_copy(r_hi[:, :], rows[:, R_X]))
        step(dve.tensor_tensor(r_lo[:, :], rows[:, R_X], r_hi[:, :].bitcast(F32), ALU.subtract))
        dve.wait_ge(gif_act, 3)
        for n in range(2):
            ins = dve.tensor_scalar(diag[:, n], ident[0:8, 0:8], decay8[:, n + 1:n + 2], None, ALU.mult)
            if n == 0:
                step(ins)
            else:
                ins.then_inc(rows_ready, 1)

        def mask_row(j, a):
            one = ident[0:8, bass.ds(2 * j + a, 1)]
            dve.tensor_scalar(rm_hi[:, :], r_hi[:, :].bitcast(F32), one, None, ALU.mult).then_inc(rm_ready, 1)
            dve.tensor_scalar(rm_lo[:, :], r_lo[:, :].bitcast(F32), one, None, ALU.mult).then_inc(rm_ready, 1)

        mask_row(0, 0)
        lo(S_QK0 + 2)
        lo(S_QK0 + 3)
        dve.wait_ge(sc_ready, 4)
        dve.wait_ge(wt_ready, 2)

        def pair(j, more):
            def weights(a):
                head = bass.ds(2 * j + a, 1)
                dve.wait_ge(scores_ready, 6 * j + (3 * a + 3))
                for n in range(3):
                    ins = dve.tensor_scalar(kw[:, n], bank[6][:, n * P:(n + 1) * P], sc[:, SC_W, n, head], None,
                                            ALU.mult)
                    ins.then_inc(kw_ready, 1)
                dve.wait_ge(isc_ready, 2 * j + (a + 1))
                for n in range(TILES):
                    ins = dve.scalar_tensor_tensor(expo[:, n * P:(n + 1) * P], bank[4][:, n * P:(n + 1) * P],
                                                   sc[:, SC_C, n, head], mask[:, :], ALU.add, ALU.add)
                    if n < TILES - 1:
                        step(ins)
                    else:
                        ins.then_inc(arg_ready, 1)
                step(dve.tensor_tensor(q_in[:, :, :], qk[:, 2 * a, P:SEQ].rearrange("p (n t) -> p n t", n=3), isc,
                                       ALU.mult))
                dve.wait_ge(exp_ready, 2 * j + (a + 1))
                dve.tensor_tensor(expo[:, :], bank[5][:, :], expo[:, :], ALU.mult).then_inc(probs_ready, 1)

            def states(a):
                for n, b in enumerate(STATE_BANK):
                    dve.wait_ge(dstate_ready, 6 * j + (3 * a + n + 1))
                    if n == 0:
                        dve.tensor_copy(state[:, 0], bank[b][:, 0:DV + 1]).then_inc(state_ready, 1)
                    else:
                        dve.wait_ge(state_ready, 6 * j + (3 * a + n))
                        dve.scalar_tensor_tensor(state[:, n], state[:, n - 1], sc[:, SC_D, n - 1, bass.ds(2 * j + a, 1)],
                                                 bank[b][:, 0:DV + 1], ALU.mult, ALU.add).then_inc(state_ready, 1)

            def z_gate(a):
                for f in range(2):
                    dve.wait_ge(silu_in, 4 * j + (16 + 2 * a + f + 1))
                    dve.scalar_tensor_tensor(tanh_z[:, f], tanh_z[:, f], 1.0, bank[2 + f][:, :], ALU.add,
                                             ALU.mult).then_inc(dve_freed, 1)
                    dve.wait_ge(dve_freed, 4 * j + (V_PAIR + 2 * a + f + 1))
                    dve.scalar_tensor_tensor(gates[:, 2 * a + f], tanh_o[:, f], 1.0, tanh_z[:, f], ALU.add,
                                             ALU.mult).then_inc(dve_step, 1)
                    own["n"] += 1

            def head_norm(a):
                dve.wait_ge(num_used, 8 * j + (4 * a + 4))
                head = bass.ds(2 * j + a, 1)
                step(dve.scalar_tensor_tensor(den[:, a], num[:, a, :, DV], -1.0, num[:, a, :, DV], ALU.mult,
                                              ALU.max))
                step(dve.tensor_tensor(den[:, a], den[:, a], sc[:, SC_E, :, head].rearrange("p n o -> p (n o)"),
                                       ALU.max))
                step(dve.reciprocal(rcp[:, a], den[:, a]))
                step(dve.tensor_tensor(rcp2[:, a], rcp[:, a], rcp[:, a], ALU.mult))
                dve.scalar_tensor_tensor(msq[:, a], ssn[:, a], 1.0 / DV, rcp2[:, a], ALU.mult, ALU.mult)\
                   .then_inc(msq_ready, 1)

            def head_scale(a):
                dve.wait_ge(head_rstd, 2 * j + (a + 1))
                step(dve.tensor_tensor(fac[:, a], rcp[:, a], msq[:, a], ALU.mult))
                for n in range(TILES):
                    dve.tensor_scalar(num[:, a, n, 0:DV], num[:, a, n, 0:DV], fac[:, a, n:n + 1], None, ALU.mult)\
                       .then_inc(hc_ready, 1)

            weights(0)
            lo(S_PAIR + 2, j, 8)
            states(0)
            lo(S_PAIR + 3, j, 8)
            z_gate(0)
            mask_row(j, 1)
            head_norm(0)
            weights(1)
            head_scale(0)
            lo(S_PAIR + 4, j, 8)
            states(1)
            lo(S_PAIR + 5, j, 8)
            z_gate(1)
            head_norm(1)
            if more:
                head_scale(1)
                mask_row(j + 1, 0)
                lo(S_PAIR + 6, j, 8)
                for a in range(2):
                    for f in range(2):
                        dve.wait_ge(yt_ready, 4 * j + (2 * a + f + 1))
                        transposed_y(4 * j + (2 * a + f), a, f)
                lo(S_PAIR + 7, j, 8)
                lo(S_PAIR + 8, j, 8)
                lo(S_PAIR + 9, j, 8)
            else:
                head_scale(1)

        PAIR_STEPS = 2 * (3 + 1 + 4 + 1 + 2) + 4 * 2
        with dve.Fori(0, 3) as j:
            enter(j, PAIR_STEPS)
            pair(j, True)
            leave(3)
        pair(3, False)
        tail(1)

    @block.tensor
    def _(pe):
        def half_ready(s, half):
            pe.wait_ge(hi_ready, 2 * s + (half + 1))
            pe.wait_ge(lo_ready, 2 * s + (half + 1))

        def feature_tile(s, r, f, b, mine=None):
            w = [t[:, r].rearrange("p (k c) -> p k c", k=KD) for t in (w_hi, w_lo)]
            for k in range(KD):
                if f == 0 and k % 4 == 0:
                    half_ready(s, k // 4)
                at = slice(f * P, (f + 1) * P)
                pe.matmul(bank[b][:, :], w[0][:, k, at], x_hi[:, k], start=(k == 0), stop=False)
                pe.matmul(bank[b][:, :], w[0][:, k, at], x_lo[:, k], start=False, stop=False)
                done = pe.matmul(bank[b][:, :], w[1][:, k, at], x_hi[:, k], start=False, stop=(k == KD - 1))
            return done

        def token_tile(s, r, t, b, left, k0, ks, start, stop, cols=SEQ, at=0):
            hi_, lo_ = left
            w = [q[:, r].rearrange("p (k c) -> p k c", k=ks) for q in (w_hi, w_lo)]
            tt = slice(t * P, (t + 1) * P)
            for k in range(ks):
                if t == 0 and at == 0 and k % (ks // 2) == 0:
                    half_ready(s, k // (ks // 2))
                c = slice(at, at + SEQ)
                pe.matmul(bank[b][:, :], hi_[:, k0 + k, tt], w[0][:, k, c], start=(start and k == 0), stop=False)
                pe.matmul(bank[b][:, :], hi_[:, k0 + k, tt], w[1][:, k, c], start=False, stop=False)
                done = pe.matmul(bank[b][:, :], lo_[:, k0 + k, tt], w[0][:, k, c], start=False,
                                 stop=(stop and k == ks - 1))
            return done

        X, Y, PP = (x_hi, x_lo), (y_hi, y_lo), (p_hi, p_lo)

        def transpose_x(e, t):
            pe.wait_ge(scaled_ready, e + 1)
            for q in range(2):
                if e % 4 >= 2:
                    pe.wait_ge(xlo_ready, 2 * (e - 2) + q + 1)
                for k in range(4):
                    done = pe.transpose(bank[norm_bank(e, t) + q][:, k * P:(k + 1) * P],
                                        scaled[:, t % 2, (4 * q + k) * P:(4 * q + k + 1) * P], ident[:, :])
                done.then_inc(xt_ready, 1)

        def v_first(s, r, e, b0, freed):
            for t in range(TILES):
                if t < TILES - 1:
                    transpose_x(e + t + 1, t + 1)
                run_v(s, r, e, b0, freed, t)

        def run_v(s, r, e, b0, freed, t):
            pe.wait_ge(xlo_ready, 2 * (e + t) + 2)
            if freed is not None:
                pe.wait_ge(act_freed, freed + t + 1)
            done = token_tile(s, r, t, b0 + t, X, 0, 4, True, False)
            if t == TILES - 1:
                done.then_inc(half_used, 1)

        def v_second(s, r, b0, ready=True):
            for t in range(TILES):
                done = token_tile(s, r, t, b0 + t, X, 4, 4, False, True)
                done.then_inc(product_ready, 1)

        pe.wait_ge(ident_ready, 1)
        transpose_x(0, 0)
        v_first(S_EV, 0, 0, 0, None)
        v_second(S_EV + 1, 1, 0)
        for t in range(TILES):
            done = token_tile(S_EV + 2, 0, t, 4 + t, X, 0, 4, True, False)
        done.then_inc(half_used, 1)
        v_second(S_EV + 3, 1, 4)

        def group_a(i):
            again = not (isinstance(i, int) and i == 0)
            for k in range(4):
                for f in range(2):
                    if not again:
                        pe.wait_ge(act_freed, A_EV + 2 * k + f + 1)
                    else:
                        if k == 0:
                            pe.wait_ge(act_freed, 2 * i + (A_EA - 2 + f + 1))
                        else:
                            pe.wait_ge(dve_freed, 6 * i + (V_EA - 6 + 2 * (k - 1) + f + 1))
                    done = feature_tile(4 * i + (S_EA + k), k % 2, f, 2 * k + f)
                    done.then_inc(product_ready, 1)

        group_a(0)
        with pe.Fori(1, 4) as i:
            group_a(i)

        pe.wait_ge(wt_ready, 1)
        pe.wait_ge(act_freed, A_EA + 8)
        with pe.Fori(0, 4) as i:
            for f in range(2):
                pe.wait_ge(dve_freed, 4 * i + (V_EB - 4 + f + 1))
                done = feature_tile(2 * i + S_EB, 0, f, f)
                done.then_inc(product_ready, 1)
            for f in range(2):
                pe.wait_ge(vst_ready, 2 * i + (f + 1))
                for n in range(TILES):
                    done = pe.matmul(bank[4 + f][:, n * P:(n + 1) * P], conv_in[:, f, n * P:(n + 1) * P],
                                     wt[:, bass.ds(2 * i + f, 1)].rearrange("p a t -> p (a t)"), start=True, stop=True)
                done.then_inc(mix_ready, 1)
            for f in range(2):
                pe.wait_ge(dve_freed, 4 * i + (V_EB - 2 + f + 1))
                done = feature_tile(2 * i + (S_EB + 1), 1, f, 2 + f)
                done.then_inc(product_ready, 1)

        def tail(l):
            s = S_OUT[l]
            for nb in range(2):
                for q in range(4):
                    if l == 0 or nb == 0 and q < 3:
                        pe.wait_ge(y_ready, 16 * l + 4 * q + 4)
                    elif q == 3:
                        pe.wait_ge(y_ready, 32)
                    sl = s + 4 * nb + q
                    for t in range(TILES):
                        if q == 0 and nb == 0 and l == 0:
                            pe.wait_ge(dve_freed, V_EB + 12 + t + 1)
                        if q == 0 and nb == 0 and l == 1:
                            if t < 2:
                                pe.wait_ge(act_freed, A_PAIR + 38 + t + 1)
                            else:
                                pe.wait_ge(dve_freed, V_PAIR + 12 + t + 1)
                        if q == 0 and nb == 1 and t >= 2:
                            pe.wait_ge(plo_ready, 2 * l + t - 1)
                        done = token_tile(sl, sl % 2, t, 4 * nb + t, Y, 4 * q, 4, q == 0, q == 3)
                        if q == 3:
                            done.then_inc(product_ready, 1)
                    if q < 3:
                        done.then_inc(half_used, 1)
                    if l == 1 and nb == 0 and q < 2:
                        pe.wait_ge(num_used, 32)
                        transpose_heads(3, q)
                if nb == 0:
                    pe.wait_ge(tail_in, 64 + 48 * l)
                    for q in range(2):
                        for t in range(TILES):
                            done = pe.transpose(bank[6 + q][:, t * P:(t + 1) * P], p_sb[:, t, q * P:(q + 1) * P],
                                                ident[:, :])
                        done.then_inc(pt_ready, 1)

            s = S_PLE[l]

            def ple_tile(nb, t):
                if nb == 0:
                    pe.wait_ge(dve_freed, V_OUT[l] + 2 * t + 1)
                else:
                    pe.wait_ge(act_freed, A_PLE[l] + PLE_ORDER.index((0, t)) + 1)
                done = token_tile(s, s % 2, t, t, PP, 0, 2, True, True, at=nb * SEQ)
                done.then_inc(product_ready, 1)
                return done

            e = 4 + 8 * l
            for nb, t in PLE_ORDER:
                ple_tile(nb, t)
                if (nb, t) == (0, 2):
                    pe.wait_ge(dve_freed, V_OUT[l] + 4)
                    transpose_x(e, 0)
                if (nb, t) == (0, 3):
                    pe.wait_ge(dve_freed, V_OUT[l] + 8)
                    transpose_x(e + 1, 1)
                if (nb, t) == (1, 2):
                    transpose_x(e + 2, 2)
            transpose_x(e + 3, 3)

            s = S_GATE[l]
            for nb in range(2):
                for q in range(2):
                    sl = s + 2 * nb + q
                    for t in range(TILES):
                        if q == 0 and nb == 0:
                            pe.wait_ge(xlo_ready, 2 * (e + t) + 2)
                            pe.wait_ge(act_freed, A_PLE[l] + PLE_ORDER.index((1, t)) + 1)
                        done = token_tile(sl, sl % 2, t, 4 * nb + t, X, 4 * q, 4, q == 0, q == 1)
                        if q == 1:
                            done.then_inc(product_ready, 1)
                        if l == 0 and nb == 1 and q == 1 and t == 2:
                            pe.wait_ge(act_freed, A_GATE[0] + 4)
                            transpose_x(8, 0)
                    if q == 0:
                        done.then_inc(half_used, 1)

        def transpose_heads(j, a):
            pe.wait_ge(hc_ready, 8 * j + (4 * a + 4))
            for f in range(2):
                b = 4 + 2 * a + f
                for n in range(TILES):
                    done = pe.transpose(bank[b][:, n * P:(n + 1) * P], num[:, a, n, f * P:(f + 1) * P], ident[:, :])
                done.then_inc(yt_ready, 1)

        tail(0)

        v_first(S_OV0, S_OV0 % 2, 8, 4, A_GATE[0] + 4)
        v_second(S_OV0 + 1, (S_OV0 + 1) % 2, 4)
        feature_tile(S_GIF, S_GIF % 2, 0, 2).then_inc(product_ready, 1)
        for a in range(2):
            s = S_QK0 + a
            if a:
                pe.wait_ge(dve_freed, V_GIF + 1)
            for f in range(2):
                done = feature_tile(s, s % 2, f, 2 * a + f)
                done.then_inc(product_ready, 1)
        pe.wait_ge(rows_ready, 1)
        pe.wait_ge(act_freed, A_OV0 + 4)
        for kind in range(3):
            for n in range(TILES):
                c = 32 * kind + 8 * n
                pe.transpose(bank[7][:, c:c + 8], tok_rows[:, kind, n * P:(n + 1) * P], ident[0:8, 0:8])
        pe.matmul(bank[7][:, 96:112], rows[:, R_ONE, 0:P], diag[:, :, :].rearrange("p n h -> p (n h)"),
                  start=True, stop=True).then_inc(rowst_ready, 1)

        def pair(j, more):
            s = 8 * j + S_PAIR

            def scores(a):
                pe.wait_ge(rm_ready, 4 * j + (2 * a + 2))
                if a:
                    pe.wait_ge(num_used, 8 * j + 4)
                else:
                    pe.wait_ge(y_ready, 4 * j + 16)
                pe.matmul(bank[4][:, :], ones8[:, :], rm_hi[:, :], start=True, stop=False)
                pe.matmul(bank[4][:, :], ones8[:, :], rm_lo[:, :], start=False, stop=True).then_inc(scores_ready, 1)
                for n in range(TILES):
                    c = slice(n * P, (n + 1) * P)
                    done = pe.matmul(bank[5][:, c], qk[:, 2 * a + 1, c], qk[:, 2 * a, c], start=True, stop=True)
                done.then_inc(scores_ready, 1)
                for n in range(3):
                    c = slice(n * P, (n + 1) * P)
                    done = pe.transpose(bank[6][:, c], qk[:, 2 * a + 1, c], ident[:, :])
                done.then_inc(scores_ready, 1)

            def dstates(a):
                pe.wait_ge(kw_ready, 6 * j + (3 * a + 3))
                for n, b in enumerate(STATE_BANK):
                    if n == 2:
                        pe.wait_ge(arg_ready, 2 * j + (a + 1))
                    pe.matmul(bank[b][:, 0:DV + 1], kw[:, n], v_odd[:, n, a], start=True, stop=True)\
                      .then_inc(dstate_ready, 1)

            def nums(a):
                pe.wait_ge(probs_ready, 2 * j + (a + 1))
                for n, b in enumerate(NUM_BANK):
                    if n:
                        pe.wait_ge(state_ready, 6 * j + (3 * a + 3))
                    done = pe.matmul(bank[b][:, 0:DV + 1], expo[:, n * P:(n + 1) * P], v_odd[:, n, a], start=True,
                                     stop=(n == 0))
                    if n:
                        done = pe.matmul(bank[b][:, 0:DV + 1], q_in[:, n - 1], state[:, n - 1], start=False, stop=True)
                    done.then_inc(num_ready, 1)

            def gate_tile(k, f, b):
                done = feature_tile(s + k, k % 2, f, b)
                done.then_inc(product_ready, 1)

            pe.wait_ge(act_freed, 12 * j + (A_PAIR - 2))
            scores(0)
            gate_tile(0, 0, 0)
            gate_tile(0, 1, 1)
            dstates(0)
            pe.wait_ge(act_freed, 12 * j + A_PAIR)
            gate_tile(1, 0, 2)
            gate_tile(1, 1, 3)
            nums(0)
            pe.wait_ge(act_freed, 12 * j + (A_PAIR + 1))
            gate_tile(2, 0, 0)
            scores(1)
            pe.wait_ge(act_freed, 12 * j + (A_PAIR + 2))
            gate_tile(2, 1, 1)
            dstates(1)
            for f in range(2):
                pe.wait_ge(dve_freed, 4 * j + (V_PAIR + f + 1))
                gate_tile(3, f, 2 + f)
            nums(1)
            if not more:
                return
            for t in range(TILES):
                if t == 0:
                    pe.wait_ge(act_freed, 12 * j + (A_PAIR + 4))
                if t == 2:
                    pe.wait_ge(dve_freed, 4 * j + (V_PAIR + 4))
                done = token_tile(s + 4, 0, t, t, X, 0, 4, True, False)
            done.then_inc(half_used, 1)
            pe.wait_ge(num_used, 8 * j + 8)
            transpose_heads(j, 0)
            transpose_heads(j, 1)
            v_second(s + 5, 1, 0)
            for a in range(2):
                for f in range(2):
                    pe.wait_ge(act_freed, 12 * j + (A_PAIR + 4 + 2 * a + f + 1))
                    done = feature_tile(s + 6 + a, a, f, 2 * a + f)
                    done.then_inc(product_ready, 1)

        with pe.Fori(0, 3) as j:
            pair(j, True)
        pair(3, False)
        tail(1)

    block.__exit__(None, None, None)


PLE_ORDER = [(0, 0), (0, 1), (0, 2), (1, 0), (1, 1), (0, 3), (1, 2), (1, 3)]
STATE_BANK = (7, 6, 4)
NUM_BANK = (5, 7, 6, 4)


def norm_bank(e, t):
    return 2 * (t % 2) + (0 if e // 4 == 2 else 4)


def pack_slots(np, even_in, even_out, odd_in, odd_out, w_ple, w_gate):
    made = []

    def feature(*blocks):
        w = np.concatenate(blocks, axis=1)
        made.append(w.reshape(KD, P, 256).transpose(1, 0, 2).reshape(P, SLOT))

    def token(w, rows, cols):
        k = rows.stop // P - rows.start // P
        made.append(w[rows, cols].reshape(k, P, SLOT // k).transpose(1, 0, 2).reshape(P, SLOT))

    def block(w, first, n=256):
        return w[:, first:first + n]

    def tail(l, w_out):
        for nb in range(2):
            for q in range(4):
                token(w_out, slice(512 * q, 512 * q + 512), slice(512 * nb, 512 * nb + 512))
        token(w_ple[l], slice(0, PLE), slice(0, D))
        for nb in range(2):
            for q in range(2):
                token(w_gate[l], slice(512 * q, 512 * q + 512), slice(512 * nb, 512 * nb + 512))

    a_b, a_c, a_x, a_gate, b_u, b_v, b_gate = [D * n for n in range(7)]
    for nb in range(2):
        for q in range(2):
            token(even_in, slice(512 * q, 512 * q + 512), slice(b_v + 512 * nb, b_v + 512 * nb + 512))
    for i in range(4):
        for first in (a_c, a_x, a_gate, a_b):
            feature(block(even_in, first + 256 * i))
    for i in range(4):
        for first in (b_gate, b_u):
            feature(block(even_in, first + 256 * i))
    tail(0, even_out)

    q0, k0, v0, o0, z0, g0 = 0, D, 2 * D, 2 * D + WIDE, 2 * D + 2 * WIDE, 2 * D + 3 * WIDE

    def pair_v(j):
        for q in range(2):
            token(odd_in, slice(512 * q, 512 * q + 512), slice(v0 + 512 * j, v0 + 512 * j + 512))

    def pair_qk(j):
        for a in range(2):
            feature(block(odd_in, q0 + P * (2 * j + a), P), block(odd_in, k0 + P * (2 * j + a), P))

    pair_v(0)
    gif = np.zeros((D, 256), odd_in.dtype)
    gif[:, 0:8] = odd_in[:, g0:g0 + 8]
    gif[:, 32:40] = odd_in[:, g0 + 8:g0 + 16]
    feature(gif)
    pair_qk(0)
    for j in range(4):
        for a in range(2):
            feature(block(odd_in, o0 + 512 * j + 256 * a))
            feature(block(odd_in, z0 + 512 * j + 256 * a))
        if j < 3:
            pair_v(j + 1)
            pair_qk(j + 1)
    tail(1, odd_out)
    assert len(made) == SLOTS
    return np.ascontiguousarray(np.stack(made))


def kernel(x, p, pre_g, post_g, ple_g, w_ple, w_ple_gate, even_w_in, even_conv_w, even_ln_g, even_ln_b,
           even_w_s, even_b_s, even_w_out, odd_w_in, odd_b_if, odd_mh_g, odd_w_out):
    import numpy as np
    import concourse.bacc as bacc
    from concourse.bass_utils import run_bass_kernel_spmd

    rows = np.stack([pre_g[0], post_g[0], ple_g[0], pre_g[1], post_g[1], ple_g[1]])
    arrays = {
        "x": x[0],
        "p": p[:, 0],
        "slots": pack_slots(np, even_w_in[0], even_w_out[0], odd_w_in[0], odd_w_out[0], w_ple, w_ple_gate),
        "g_rows": rows,
        "ln_rows": np.stack([even_ln_g[0], even_ln_b[0]]),
        "w_mix": even_w_s[0].transpose(2, 0, 1),
        "b_mix": even_b_s[0].T.reshape(1, 8 * P),
        "conv_w": even_conv_w[0].reshape(3, 8, P).transpose(2, 0, 1),
        "gate_bias": odd_b_if[0].reshape(16, 1),
        "head_g": odd_mh_g[0].reshape(16, P).T,
    }
    arrays = {n: np.ascontiguousarray(a) for n, a in arrays.items()}
    nc = bacc.Bacc("TRN2", target_bir_lowering=False, num_devices=1, dynamic_dma_scratch_size=1024)
    args = [nc.dram_tensor(f"in_{n}", a.shape, mybir.dt.from_np(a.dtype), kind="ExternalInput").ap()
            for n, a in arrays.items()]
    out = nc.dram_tensor("out_0", (SEQ, D), F32, kind="ExternalOutput").ap()
    trunk(nc, *args, out)
    r = run_bass_kernel_spmd(nc, [{f"in_{n}": a for n, a in arrays.items()}], core_ids=[0])
    return r.results[0]["out_0"].reshape(1, SEQ, D)
```
